# Optimizing a Trainium2 kernel written in Bass

```python
import math
import jax, jax.numpy as jnp
from jax import lax
import numpy as np

D_MODEL = 1024
BATCH = 1
SEQ = 2048
DEPTH = 1

D_MIX = D_MODEL
A_HEADS = 4
A_HEAD_DIM = 128
A_WIDTH = A_HEADS * A_HEAD_DIM
CONV_K = 4
CHUNK = 64
B_Q_HEADS = 8
B_KV_HEADS = 2
B_HEAD_DIM = 64
B_GROUP = B_Q_HEADS // B_KV_HEADS
B_WIDTH = B_Q_HEADS * B_HEAD_DIM
B_KV_WIDTH = B_KV_HEADS * B_HEAD_DIM
WINDOW = 128
BLOCK = 128
IN_SIZES = (A_WIDTH, A_WIDTH, A_WIDTH, A_WIDTH, A_HEADS, A_HEADS,
            B_WIDTH, B_KV_WIDTH, B_KV_WIDTH, B_WIDTH)
IN_COLS = sum(IN_SIZES)
DEEPNORM_ALPHA = (2 * DEPTH) ** 0.25
DEEPNORM_BETA = (8 * DEPTH) ** -0.25
LN_EPS = 1e-5
RMS_EPS = 1e-6
L2_EPS = 1e-6

kernel_name = "hybrid_deltanet_swa_sink_alibi_deepnorm"

def _alibi_slopes(n_heads):
    return jnp.asarray([2.0 ** (-8.0 * (h + 1) / n_heads) for h in range(n_heads)], dtype=jnp.float32)

def _layernorm(x, g, b):
    xf = x.astype(jnp.float32)
    mu = jnp.mean(xf, axis=-1, keepdims=True)
    var = jnp.mean(jnp.square(xf - mu), axis=-1, keepdims=True)
    y = (xf - mu) * lax.rsqrt(var + LN_EPS) * g.astype(jnp.float32) + b.astype(jnp.float32)
    return y.astype(x.dtype)

def _l2norm(t):
    return t * lax.rsqrt(jnp.sum(jnp.square(t), axis=-1, keepdims=True) + L2_EPS)

def _short_conv(x, w):
    c = x.shape[-1]
    return lax.conv_general_dilated(
        x, w[:, None, :].astype(x.dtype), window_strides=(1,), padding=[(CONV_K - 1, 0)],
        dimension_numbers=('NWC', 'WIO', 'NWC'), feature_group_count=c)

def _gated_delta_rule(q, k, v, g, beta):
    bsz, t_len, h, dk = q.shape
    dv = v.shape[-1]
    n = t_len // CHUNK

    def chunks(t):
        t = t.reshape((bsz, n, CHUNK, h) + t.shape[3:])
        return jnp.moveaxis(t, 3, 1)

    q, k, v, g, beta = chunks(q), chunks(k), chunks(v), chunks(g), chunks(beta)
    g = jnp.cumsum(g, axis=-1)
    causal = jnp.tril(jnp.ones((CHUNK, CHUNK), dtype=bool))
    strict = jnp.tril(jnp.ones((CHUNK, CHUNK), dtype=bool), -1)
    decay = jnp.exp(jnp.where(causal, g[..., :, None] - g[..., None, :], -jnp.inf))
    k_beta = k * beta[..., None]
    a_mat = jnp.where(strict, jnp.einsum('bhncd,bhnsd->bhncs', k_beta, k) * decay, 0.0)
    eye = jnp.eye(CHUNK, dtype=a_mat.dtype)
    t_mat = lax.linalg.triangular_solve(eye + a_mat, jnp.broadcast_to(eye, a_mat.shape),
                                        left_side=True, lower=True)
    u = jnp.einsum('bhncs,bhnse->bhnce', t_mat, v * beta[..., None])
    w = jnp.einsum('bhncs,bhnsd->bhncd', t_mat, k_beta * jnp.exp(g)[..., None])
    qk = jnp.where(causal, jnp.einsum('bhncd,bhnsd->bhncs', q, k) * decay, 0.0)
    q_dec = q * jnp.exp(g)[..., None]
    k_dec = k * jnp.exp(g[..., -1:] - g)[..., None]
    g_tot = jnp.exp(g[..., -1])
    xs = tuple(jnp.moveaxis(t, 2, 0) for t in (q_dec, k_dec, u, w, qk, g_tot))

    def step(s, inp):
        q_c, k_c, u_c, w_c, qk_c, gt = inp
        v_new = u_c - jnp.einsum('bhcd,bhde->bhce', w_c, s)
        o = jnp.einsum('bhcd,bhde->bhce', q_c, s) + jnp.einsum('bhcs,bhse->bhce', qk_c, v_new)
        s = s * gt[..., None, None] + jnp.einsum('bhcd,bhce->bhde', k_c, v_new)
        return s, o

    s0 = jnp.zeros((bsz, h, dk, dv), jnp.float32)
    _, o = lax.scan(step, s0, xs)
    o = jnp.moveaxis(o, 0, 2)
    return jnp.moveaxis(o, 1, 3).reshape(bsz, t_len, h, dv)

def _deltanet_group(q, k, v, z, b, a, conv_w, a_log, dt_bias, norm_w):
    bsz, t_len, _ = q.shape
    qkv = jax.nn.silu(_short_conv(jnp.concatenate([q, k, v], axis=-1), conv_w))
    q, k, v = jnp.split(qkv, 3, axis=-1)
    heads = lambda t: t.reshape(bsz, t_len, A_HEADS, A_HEAD_DIM).astype(jnp.float32)
    q = _l2norm(heads(q)) * (A_HEAD_DIM ** -0.5)
    k = _l2norm(heads(k))
    v = heads(v)
    beta = jax.nn.sigmoid(b.astype(jnp.float32))
    g = -jnp.exp(a_log.astype(jnp.float32)) * jax.nn.softplus(
        a.astype(jnp.float32) + dt_bias.astype(jnp.float32))
    o = _gated_delta_rule(q, k, v, g, beta)
    o = o * lax.rsqrt(jnp.mean(jnp.square(o), axis=-1, keepdims=True) + RMS_EPS) * norm_w.astype(jnp.float32)
    return o.reshape(bsz, t_len, A_WIDTH).astype(z.dtype) * jax.nn.silu(z)

def _swa_group(q, k, v, z, sinks):
    bsz, t_len, _ = q.shape
    n = t_len // BLOCK
    q = q.reshape(bsz, n, BLOCK, B_KV_HEADS, B_GROUP, B_HEAD_DIM)
    k = k.reshape(bsz, t_len, B_KV_HEADS, B_HEAD_DIM)
    v = v.reshape(bsz, t_len, B_KV_HEADS, B_HEAD_DIM)

    def band(t):
        prev = jnp.pad(t, ((0, 0), (BLOCK, 0), (0, 0), (0, 0)))[:, :t_len]
        shp = (bsz, n, BLOCK, B_KV_HEADS, B_HEAD_DIM)
        return jnp.concatenate([prev.reshape(shp), t.reshape(shp)], axis=2)

    kb, vb = band(k), band(v)
    s = jnp.einsum('bnqhgd,bnshd->bhgnqs', q, kb).astype(jnp.float32) * (B_HEAD_DIM ** -0.5)
    q_idx = jnp.arange(BLOCK)[:, None]
    s_idx = jnp.arange(2 * BLOCK)[None, :]
    dist = q_idx + BLOCK - s_idx
    key_pos = jnp.arange(n)[:, None] * BLOCK - BLOCK + jnp.arange(2 * BLOCK)[None, :]
    mask = ((dist >= 0) & (dist < WINDOW))[None] & (key_pos >= 0)[:, None, :]
    slopes = _alibi_slopes(B_Q_HEADS).reshape(B_KV_HEADS, B_GROUP)
    s = s - slopes[:, :, None, None, None] * dist.astype(jnp.float32)
    s = jnp.where(mask, s, -jnp.inf)
    sink = sinks.astype(jnp.float32).reshape(B_KV_HEADS, B_GROUP)[:, :, None, None]
    m = jnp.maximum(jnp.max(s, axis=-1), sink)
    p = jnp.exp(s - m[..., None])
    p = p / (jnp.sum(p, axis=-1, keepdims=True) + jnp.exp(sink - m)[..., None])
    o = jnp.einsum('bhgnqs,bnshd->bnqhgd', p.astype(vb.dtype), vb)
    return o.reshape(bsz, t_len, B_WIDTH) * jax.nn.silu(z)

def _layer(x, w_in, conv_w, a_log, dt_bias, norm_w, sinks, w_out, ln_g, ln_b):
    h = jnp.einsum('btd,dc->btc', x, w_in)
    offsets = [sum(IN_SIZES[:i]) for i in range(1, len(IN_SIZES))]
    qa, ka, va, za, ba, aa, qb, kb, vb, zb = jnp.split(h, offsets, axis=-1)
    ya = _deltanet_group(qa, ka, va, za, ba, aa, conv_w, a_log, dt_bias, norm_w)
    yb = _swa_group(qb, kb, vb, zb, sinks)
    y = jnp.einsum('btc,cd->btd', jnp.concatenate([ya, yb], axis=-1), w_out)
    return _layernorm(DEEPNORM_ALPHA * x + y, ln_g, ln_b)

def setup_inputs(seed: int = 0) -> dict:
    key = jax.random.key(seed)
    ks = jax.random.split(key, 10)
    x = jax.random.normal(ks[0], (BATCH, SEQ, D_MODEL), jnp.float32)
    col_scale = np.concatenate([
        np.ones(2 * A_WIDTH), np.full(A_WIDTH, DEEPNORM_BETA), np.ones(A_WIDTH + 2 * A_HEADS),
        np.ones(B_WIDTH + B_KV_WIDTH), np.full(B_KV_WIDTH, DEEPNORM_BETA), np.ones(B_WIDTH)]).astype(np.float32)
    w_in = jax.random.normal(ks[1], (DEPTH, D_MODEL, IN_COLS), jnp.float32) * (D_MODEL ** -0.5) * jnp.asarray(col_scale)
    conv_w = jax.random.normal(ks[2], (DEPTH, CONV_K, 3 * A_WIDTH), jnp.float32) * (CONV_K ** -0.5)
    a_log = jnp.log(jax.random.uniform(ks[3], (DEPTH, A_HEADS), jnp.float32, 1.0, 16.0))
    dt = jnp.exp(jax.random.uniform(ks[4], (DEPTH, A_HEADS), jnp.float32, math.log(1e-3), math.log(1e-1)))
    dt_bias = dt + jnp.log(-jnp.expm1(-dt))
    norm_w = 1.0 + 0.02 * jax.random.normal(ks[5], (DEPTH, A_HEAD_DIM), jnp.float32)
    sinks = 0.5 * jax.random.normal(ks[6], (DEPTH, B_Q_HEADS), jnp.float32)
    w_out = jax.random.normal(ks[7], (DEPTH, D_MIX, D_MODEL), jnp.float32) * (D_MIX ** -0.5) * DEEPNORM_BETA
    ln_g = 1.0 + 0.02 * jax.random.normal(ks[8], (DEPTH, D_MODEL), jnp.float32)
    ln_b = 0.02 * jax.random.normal(ks[9], (DEPTH, D_MODEL), jnp.float32)
    return {"x": x, "w_in": w_in, "conv_w": conv_w, "a_log": a_log, "dt_bias": dt_bias,
            "norm_w": norm_w, "sinks": sinks, "w_out": w_out, "ln_g": ln_g, "ln_b": ln_b}

def reference(x, w_in, conv_w, a_log, dt_bias, norm_w, sinks, w_out, ln_g, ln_b):
    for l in range(DEPTH):
        x = _layer(x, w_in[l], conv_w[l], a_log[l], dt_bias[l], norm_w[l], sinks[l],
                   w_out[l], ln_g[l], ln_b[l])
    return x


_drawn_inputs = setup_inputs


def setup_inputs(seed=0):
    import zlib

    import numpy as np

    out = dict(_drawn_inputs(seed))
    spreads = {}
    factors = {'norm_w': 23.83, 'sinks': 36.698, 'ln_g': 8.98, 'ln_b': 8.558}
    for name, (base, spread) in spreads.items():
        noise = np.random.default_rng([zlib.crc32(name.encode()), seed]).standard_normal(out[name].shape)
        drawn = base * np.exp(spread * noise) if base else spread * noise
        out[name] = __import__('jax').numpy.asarray(drawn.astype(out[name].dtype))
    for name, factor in factors.items():
        out[name] = (out[name] * factor).astype(out[name].dtype)
    return out
```

```python
from contextlib import ExitStack

import numpy as np

import concourse.bass as bass
from concourse import mybir

F32 = mybir.dt.float32
F32R = mybir.dt.float32r
U8 = mybir.dt.uint8
ALU = mybir.AluOpType
ACT = mybir.ActivationFunctionType

P = 128
T = 2048
D = 1024
KT = D // P
AH = 4
CONV = 4
UNIT = 512
SBS = T // UNIT
CH = UNIT // P
NT = T // P
LEVELS = 6
PAIRS = 4
BD = 64
ALPHA = 2.0 ** 0.25
LN_EPS, RMS_EPS, L2_EPS = 1e-5, 1e-6, 1e-6
MASKED = -(2.0 ** 100)
LOWEST = -3.0e38
EXP_LN_SET = "natural_log_exp_and_others"
N_CONST = 10
SPLIT_PARTS = ((0, 0), (0, 1), (1, 0))
COPY_AT = {4: [[0], [], [1], [2, 3]], 2: [[], [], [0], [1]], 0: [[]] * 4}
START_FILL = (7, 8, 5, 2)
LEVEL_FILL = [[(0, 2), (1, 2)], [(1, 4)], [(1, 4)], [(1, 5)], [(1, 5)], [(1, 4)],
              [(2, 4)], [(2, 4)], [(2, 4)], [(2, 4)], [(2, 4)], []]
STEP_FILL = [([(2, 4)], [(3, 3)], [(3, 1)])] + [([(3, 2)], [(3, 3)], [(3, 1)])] * (CH - 1)
END_FILL = 2
RAW_COPY_AT = (0, 2, 5)
CONV_AT = [[], [(0, 0), (0, 1)], [(0, 2), (0, 3)], [(1, 0), (1, 1)], [(1, 2), (1, 3)], []]
V_CONV_AT = [(0, 1), (1, 2), (1, 2), (1, 0)]


class Counter:

    def __init__(self, sem, per, start=0):
        self.sem, self.per, self.start = sem, per, start

    def at(self, slot, k):
        h, sb = slot
        return h * (SBS * self.per) + (self.start + sb * self.per + k)


def n_keys(j, s, i):
    return P if s == 0 and i == 0 else 2 * P


def next_slot(slot):
    h, sb = slot
    return (h, sb + 1) if sb < SBS - 1 else (h + 1, 0)


def build_layer(nc, xT, x, w_in, w_ba, conv_w, a_log, dt_bias, norm_w, sinks, w_out, ln_g, ln_b,
                c_tri, c_ident, c_masks, c_dist, c_slope, y_spill, g_rows, out):
    ctx = ExitStack()
    with ctx:
        def sb(name, shape, dt=F32):
            return ctx.enter_context(nc.sbuf_tensor(name, shape, dt))

        def sem(name):
            return ctx.enter_context(nc.semaphore(name))

        def counter(name, per):
            return Counter(sem(name), per)

        from_one = []

        def sem_from_one(name):
            from_one.append(sem(name))
            return from_one[-1]

        def counter_from_one(name, per):
            return Counter(sem_from_one(name), per, start=1)

        bank = [ctx.enter_context(nc.psum_tensor(f"bank{i}", [P, 512], F32)) for i in range(8)]
        dense_bank = bank[0:2]
        half_bank = bank[2:4]
        turn_bank = bank[4:6]

        xr = sb("xr", [P, 2, KT, T], F32R)
        w = sb("w", [P, 4, 2, KT, P], F32R)
        w_raw = sb("w_raw", [P, 2, KT * P])
        ident = sb("ident", [P, P])
        tri = sb("tri", [P, P])
        eps = sb("eps", [P, 2])
        closed = sb("closed", [P, P])
        masks = sb("masks", [P, 1 + LEVELS, P], U8)
        first, levels = masks[:, 0], masks[:, 1:]
        ones = sb("ones", [P, P])
        convw_all = sb("convw_all", [P, AH + 1, 3, CONV])
        convw = sb("convw", [P, 3, CONV])
        normw = sb("normw", [P, 1])
        dtb = sb("dtb", [P, AH])
        alog = sb("alog", [P, AH])
        ba_raw = sb("ba_raw", [P, KT, 2 * AH])
        ba_w = sb("ba_w", [P, 2, KT, 2 * AH], F32R)
        G_, EG, BETA, NBETA, EKD, EGT = range(6)
        cols_all = sb("cols_all", [P, AH, 6, NT])
        cols = sb("cols", [P, 6, NT])
        sums_sq = sb("sums_sq", [P, 2, CH])
        conv_in = sb("conv_in", [P, 3, CONV - 1 + UNIT])
        kq = sb("kq", [P, 2, 2, UNIT])
        v_ch = sb("v_ch", [P, UNIT])
        z_raw = sb("z_raw", [P, UNIT])
        gate = sb("gate", [P, UNIT])
        np_buf = sb("np_buf", [P, 2, CH, P])
        n_buf, p_buf = np_buf[:, 0], np_buf[:, 1]
        work = sb("work", [P, 8, CH, P])
        decay, pt, y_inv, t_inv, k_dec, beta_v, o_tok, o_scaled = (work[:, i] for i in range(8))
        x_stage = [work[:, 2 * i:2 * i + 2].rearrange("p a t n -> p a (t n)") for i in range(4)]
        state = sb("state", [P, P])
        resid = sb("resid", [P, P])
        v_new = sb("v_new", [P, P])
        q_state = sb("q_state", [P, P])
        y_out = sb("y_out", [P, 2, UNIT])
        masks_raw = y_out[:].rearrange("p a n -> p (a n)")[:, 0:(1 + LEVELS) * P]
        pre = gate[:, 0:7 * AH * NT].rearrange("p (a h t) -> p a h t", a=7, h=AH)
        ba_ch = work[0:2 * AH, 4:8].rearrange("p a t n -> p (a t n)")
        g_turned = work[0:AH * NT, 7, 0]
        ea = sb("ea", [P, AH])
        ln_ss = sb("ln_ss", [P, 2, CH])
        r_k = sb("r_k", [P, CH])
        rq2 = sb("rq2", [P, CH])
        col_s = sb("col_s", [P, CH])
        nb_rk = sb("nb_rk", [P, CH])
        w_ks = sb("w_ks", [P, CH])
        kd_s = sb("kd_s", [P, CH])
        ss_o = sb("ss_o", [P, CH])
        rms_in = sb("rms_in", [P, CH])
        rms_ln = sb("rms_ln", [P, CH])
        rms_sum = sb("rms_sum", [P, CH])
        o_scale = sb("o_scale", [P, CH])

        k_ch = work[:, 0:4].rearrange("p a t n -> p (a t n)")
        v_tok = work[:, 4:8].rearrange("p a t n -> p (a t) n")
        q_in = [kq[:, i, 0] for i in range(2)]
        z_in = [kq[:, i, 1] for i in range(2)]
        score = conv_in[:].rearrange("p a n -> p (a n)")[:, 0:4 * 256].rearrange("p (r h n) -> p r h n", r=2, h=2)
        p_turned = [np_buf[:, i] for i in range(2)]
        bias = z_raw[:].rearrange("p (h n) -> p h n", h=2)
        dist = cols_all[:].rearrange("p h c t -> p (h c t)")[:, 0:2 * P]
        SLOPE, SINK, NSINK = range(3)
        pair_all = sb("pair_all", [P, PAIRS, 3, 2])
        pair = sb("pair", [P, 3, 2])
        row_max = sb("row_max", [P, CH, 2])
        neg_max = sb("neg_max", [P, CH, 2])
        row_sum = sb("row_sum", [P, CH, 2])
        sink_in = sb("sink_in", [P, CH, 2])
        sink_exp = sb("sink_exp", [P, CH, 2])
        denom = sb("denom", [P, CH, 2])
        denom_inv = sb("denom_inv", [P, CH, 2])
        wo_rows = [xr[:, :, 2 * (k % 4):2 * (k % 4) + 2, (k // 4) * UNIT:(k // 4 + 1) * UNIT] for k in range(KT)]
        y_split = [xr[:, :, :, D + i * P:D + (i + 1) * P] for i in range(2)]
        y_tile = [w_raw[:, i].rearrange("p (k n) -> p k n", n=P) for i in range(2)]
        x_tile = [work[:, 4 + 2 * i:6 + 2 * i].rearrange("p a t n -> p (a t n)") for i in range(2)]
        res = [kq[:, i].rearrange("p a n -> p (a n)") for i in range(2)]
        gain = np_buf[:].rearrange("p a t n -> p (a t n)")
        shift = conv_in[:].rearrange("p a n -> p (a n)")[:, 0:D]
        stats = sb("stats", [P, 2, 6])
        moments = sb("moments", [P, 2])
        ln_var = sb("ln_var", [P, 1])
        rstd = sb("rstd", [P, 1])

        passed = {nc.sync: sem("sync_passed"), nc.gpsimd: sem("gpsimd_passed"), nc.vector: sem("vector_passed")}
        const_in = sem("const_in")
        const_ready = sem("const_ready")
        masks_ready = sem("masks_ready")
        x_in = [sem(f"x_in{i}") for i in range(4)]
        x_high = sem("x_high")
        x_split = sem("x_split")
        ba_projected = sem("ba_projected")
        ba_copied = sem("ba_copied")
        ba_done = sem("ba_done")
        pre_act = sem("pre_act")
        pre_dve = sem("pre_dve")
        g_ready = sem("g_ready")
        g_sums = sem("g_sums")
        g_diff = sem("g_diff")
        w_landed = [sem(f"w_landed{i}") for i in range(2)]
        w_high = sem("w_high")
        w_ready = sem("w_ready")
        dense_done = counter("dense_done", 4)
        raw_copied = counter("raw_copied", 4)
        conv_step = counter("conv_step", 3 + 3 + 7)
        conv_ready = counter("conv_ready", 3)
        tail_saved = counter("tail_saved", 3)
        prep_ready = counter("prep_ready", 2)
        gate_ready = counter("gate_ready", 1)
        qtok_done = counter("qtok_done", 1)
        kk_done = counter("kk_done", 2)
        ktok_done = counter("ktok_done", 1)
        vtok_done = counter("vtok_done", 1)
        zt_done = counter("zt_done", 2)
        y1_done = counter("y1_done", 2)
        p_done = counter("p_done", 2 * LEVELS)
        yy_done = counter("yy_done", 2 * LEVELS)
        turn_done = counter("turn_done", 2 * (LEVELS - 1))
        ks_done = counter("ks_done", CH)
        qs_done = counter("qs_done", CH)
        tr_done = counter("tr_done", CH)
        kv_done = counter("kv_done", CH)
        o_done = counter("o_done", CH)
        ot_done = counter("ot_done", 1)
        ln_ready = counter("ln_ready", 2)
        rk_ready = counter("rk_ready", 2)
        decay_ready = counter("decay_ready", 1)
        y1_copied = counter("y1_copied", 2)
        p_copied = counter("p_copied", 2 * LEVELS)
        t_copied = counter_from_one("t_copied", 2 * (LEVELS - 1))
        rms_ln_ready = counter("rms_ln_ready", 1)
        o_scale_ready = counter("o_scale_ready", 1)
        cols_staged = sem("cols_staged")
        g_copied = sem("g_copied")
        g_turn_done = sem("g_turn_done")
        g_turned_ready = sem("g_turned_ready")
        g_stored = sem("g_stored")
        g_row_in = counter("g_row_in", 16)
        convw_staged = sem("convw_staged")
        gdiff_ready = counter("gdiff_ready", CH)
        small = counter("small", 6)
        beta_v_ready = counter("beta_v_ready", 1)
        k_dec_ready = counter("k_dec_ready", 1)
        zp_ready = counter("zp_ready", 4)
        n_ready = counter("n_ready", 2)
        t1_ready = counter("t1_ready", 2)
        y_ready = counter_from_one("y_ready", 2 * LEVELS)
        t_cleared = counter("t_cleared", 1)
        state_zeroed = sem("state_zeroed")
        state_ready = counter_from_one("state_ready", CH)
        resid_ready = counter("resid_ready", CH)
        q_state_ready = counter("q_state_ready", CH)
        v_new_ready = counter("v_new_ready", CH)
        o_ready = counter("o_ready", CH)
        ss_ready = counter("ss_ready", CH)
        kq_ss_ready = counter("kq_ss_ready", 2 * CH)
        o_scaled_ready = counter("o_scaled_ready", 1)
        y_out_ready = counter_from_one("y_out_ready", 1)
        y_spilled = [sem_from_one(f"y_spilled{i}") for i in range(2)]
        moved = sem("moved")
        dist_in = sem("dist_in")
        vt_done = counter("vt_done", 1)
        vt_copied = counter("vt_copied", 1)
        score_done = counter("score_done", 2 * CH)
        max_ready = counter("max_ready", 2 * CH)
        nmax_ready = counter("nmax_ready", CH)
        exp_ready = counter("exp_ready", 2 * CH)
        p_turn_done = counter("p_turn_done", CH)
        p_turned_ready = counter("p_turned_ready", CH)
        pv_done = counter("pv_done", CH)
        sink_in_ready = counter("sink_in_ready", CH)
        sink_exp_ready = counter("sink_exp_ready", CH)
        denom_step = counter("denom_step", 2 * CH)
        p_scaled = counter("p_scaled", 2 * CH)
        gate_b_ready = counter("gate_b_ready", 1)
        y_b_ready = counter("y_b_ready", 1)
        pair_staged = sem("pair_staged")
        bias_ready = sem("bias_ready")
        wo_high = sem("wo_high")
        wo_split = sem("wo_split")
        gb_in = sem("gb_in")
        y_in = [sem(f"y_in{i}") for i in range(2)]
        xt_in = [sem(f"xt_in{i}") for i in range(2)]
        y_high = sem("y_high")
        y_low = sem("y_low")
        proj_done = sem("proj_done")
        res_ready = sem("res_ready")
        stats_ready = sem("stats_ready")
        moments_ready = sem("moments_ready")
        var_ready = sem("var_ready")
        rstd_ready = sem("rstd_ready")
        normed = sem("normed")
        scaled = sem("scaled")
        shifted = sem("shifted")
        out_sent = [sem_from_one(f"out_sent{i}") for i in range(2)]

        def halves(buf):
            return [buf[:, 0:2], buf[:, 2:4]]

        def tiles(b, n=CH):
            return b[:, 0:n * P].rearrange("p (t n) -> p t n", n=P)

        def per_tile(col, n=CH):
            return col.unsqueeze(2).to_broadcast([P, n, P])

        def settle(engine):
            engine.sem_inc(passed[engine], 1)

        def dense(c, sbn, steps, place=None):
            place = c if place is None else place
            for s in steps:
                k, part = divmod(s, 3)
                wp, xp = SPLIT_PARTS[part]
                ins = nc.tensor.matmul(dense_bank[c % 2][:], w[:, place, wp, k, :],
                                       xr[:, xp, k, sbn * UNIT:(sbn + 1) * UNIT],
                                       start=(s == 0), stop=(s == 3 * KT - 1))
            return ins

        def count_b(unit, c):
            j, s = unit
            if type(j) is int and j == 0:
                return 64 + 4 * s + c + 1
            return j * 8 + (72 + 2 * s + c + 1)

        def next_tiles(j, s):
            nxt = next_slot((j, s))
            if type(j) is int and j == 0 and s < SBS - 1:
                return nxt, [(0, "k"), (1, "v"), (2, "q"), (3, "z")]
            if type(j) is int and j == PAIRS - 1 and s == SBS - 1:
                return nxt, []
            return nxt, [(0, "q"), (1, "z")]

        def attention_units(engine, program):
            for s in range(SBS):
                program(0, s)
            with engine.Fori(1, PAIRS - 1) as j:
                for s in range(SBS):
                    program(j, s)
            for s in range(SBS):
                program(PAIRS - 1, s)

        block = ctx.enter_context(nc.Block())
        @block.sync
        def _(sp):
            for one in from_one:
                sp.sem_inc(one, 1)
            def load_x(n):
                sbn, k2 = divmod(n, 4)
                if n >= 4:
                    sp.wait_ge(x_split, n - 3)
                sp.dma_start(x_stage[n % 4],
                             xT[2 * k2 * P:(2 * k2 + 2) * P, sbn * UNIT:(sbn + 1) * UNIT]
                             .rearrange("(k p) t -> p k t", p=P)).then_inc(x_in[n % 4], 16)

            def load_w(c, tile):
                sp.dma_start(w_raw[:, c % 2], tile).then_inc(w_landed[c % 2], 16)

            load_w(0, w_in[0])
            load_x(0)
            load_x(1)
            load_w(1, w_in[1])
            load_x(2)
            load_x(3)
            for n in range(2, 4):
                sp.wait_ge(w_ready, n - 1)
                load_w(n, w_in[n])
            for n in range(4, 16):
                load_x(n)
            sp.wait_ge(g_turned_ready, 1)
            sp.dma_start(g_rows[0:AH * NT], g_turned).then_inc(g_stored, 16)
            sp.dma_start(g_rows[AH * NT:(AH + 1) * NT], g_turned[0:NT]).then_inc(g_stored, 16)
            with sp.Fori(0, AH) as h:
                def load_next_w(c):
                    sp.wait_ge(w_ready, h * 4 + (4 + c - 1))
                    settle(sp)
                    load_w(c, w_in[bass.ds(h * 4 + (4 + c), 1)].rearrange("a p n -> (a p) n"))

                def store_y(s):
                    sp.wait_ge(y_out_ready.sem, y_out_ready.at((h, s), 1))
                    settle(sp)
                    sp.dma_start(y_spill[bass.ds(h, 1), :, s * UNIT:(s + 1) * UNIT].rearrange("a p n -> (a p) n"),
                                 y_out[:, s % 2]).then_inc(y_spilled[s % 2], 16)

                load_next_w(0)
                load_next_w(1)
                store_y(0)
                store_y(1)
                load_next_w(2)
                load_next_w(3)
                store_y(2)
                store_y(3)

            sp.wait_ge(y_out_ready.sem, y_out_ready.at((AH, 0), 0))
            sp.dma_start(dist, c_dist).then_inc(dist_in, 16)

            def attention_unit(j, s):
                if s == 0 and not (type(j) is int and j == PAIRS - 1):
                    for c in range(2):
                        sp.wait_ge(w_ready, j * 2 + (19 + c))
                        settle(sp)
                        load_w(c, w_in[bass.ds(j * 2 + (20 + c), 1)].rearrange("a p n -> (a p) n"))
                if type(j) is int and j == PAIRS - 1:
                    for k in ((0, 1), (2, 3, 4, 5), (6, 7), ())[s]:
                        load_wo(k)
                    if s == SBS - 1:
                        sp.wait_ge(y_spilled[0], 16 * 15 + 1)
                        for i in range(2):
                            sp.wait_ge(wo_split, KT - 1 + i)
                            load_y_tile(i, i)
                sp.wait_ge(y_b_ready.sem, y_b_ready.at((j, s), 1))
                settle(sp)
                sp.dma_start(y_spill[bass.ds(j + AH, 1), :, s * UNIT:(s + 1) * UNIT].rearrange("a p n -> (a p) n"),
                             y_out[:, s % 2]).then_inc(y_spilled[s % 2], 16)

            def load_wo(k):
                if k < 2:
                    sp.wait_ge(w_ready, 25 + k)
                else:
                    sp.wait_ge(wo_split, k - 1)
                sp.dma_start(w_raw[:, k % 2], w_out[k]).then_inc(w_landed[k % 2], 16)

            y_tiles = y_spill.rearrange("c p (t n) -> t p c n", n=P)

            def load_y_tile(t, i):
                sp.dma_start(y_tile[i], y_tiles[bass.ds(t, 1)].rearrange("a p c n -> (a p) c n")).then_inc(y_in[i], 16)

            def load_x_tile(t, i):
                sp.dma_start(x_tile[i], x[bass.ds(t * P, P)]).then_inc(xt_in[i], 16)

            attention_units(sp, attention_unit)
            for i in range(2):
                sp.wait_ge(y_spilled[i], 16 * 16 + 1)
            for i in range(2):
                load_x_tile(i, i)
            sp.dma_start(gain, ln_g).then_inc(gb_in, 16)
            sp.dma_start(shift, ln_b).then_inc(gb_in, 16)

            def store_tile(t2, i):
                t = t2 * 2 + i
                sp.wait_ge(shifted, t + 1)
                settle(sp)
                sp.dma_start(out[bass.ds(t * P, P)], res[i]).then_inc(out_sent[i], 16)

            with sp.Fori(0, NT // 2 - 1) as t2:
                for i in range(2):
                    sp.wait_ge(y_low, t2 * 2 + (i + 1))
                    settle(sp)
                    load_y_tile(t2 * 2 + (2 + i), i)
                for i in range(2):
                    sp.wait_ge(res_ready, t2 * 4 + (2 * i + 2))
                    settle(sp)
                    load_x_tile(t2 * 2 + (2 + i), i)
                for i in range(2):
                    store_tile(t2, i)
            for i in range(2):
                store_tile(NT // 2 - 1, i)
            for i in range(2):
                sp.wait_ge(out_sent[i], 16 * NT // 2 + 1)

        @block.gpsimd
        def _(pool):
            def split(c, landed, count):
                hi = w[:, c, 0].rearrange("p k n -> p (k n)")
                lo = w[:, c, 1].rearrange("p k n -> p (k n)")
                pool.wait_ge(w_landed[c % 2], landed)
                settle(pool)
                nc.gpsimd.tensor_scalar(hi, w_raw[:, c % 2], 1.0, None, ALU.mult).then_inc(w_high, 1)
                pool.wait_ge(w_high, count)
                nc.gpsimd.tensor_tensor(lo, w_raw[:, c % 2], hi, ALU.subtract).then_inc(w_ready, 1)

            for n in range(4):
                split(n, 16 * (n // 2 + 1), n + 1)
            pool.wait_ge(const_in, 16 * N_CONST)
            pool.wait_ge(x_split, 16)
            with pool.Fori(0, AH) as h:
                def clear_t(s):
                    pool.wait_ge(y_ready.sem, y_ready.at((h, s), 0))
                    settle(pool)
                    nc.gpsimd.tensor_copy(t_inv, ident[:].unsqueeze(1).to_broadcast([P, CH, P]))\
                        .then_inc(t_cleared.sem, 1)

                def split_next(c):
                    pool.wait_ge(dense_done.sem, dense_done.at((h, 3), c + 1))
                    split(c, h * 32 + 16 * (2 + c // 2 + 1), h * 4 + (4 + c + 1))

                clear_t(0)
                clear_t(1)
                clear_t(2)
                split_next(0)
                split_next(1)
                split_next(2)
                clear_t(3)
                split_next(3)

            for c in range(2):
                pool.wait_ge(dense_done.sem, count_b((0, SBS - 1), c))
                split(c, 16 * 11, 21 + c)
            with pool.Fori(1, PAIRS - 1) as j:
                for c in range(2):
                    pool.wait_ge(dense_done.sem, count_b((j, SBS - 1), c))
                    split(c, j * 16 + 16 * 11, j * 2 + (21 + c))
            for k in range(KT):
                pool.wait_ge(w_landed[k % 2], 16 * (14 + k // 2))
                pool.wait_ge(dense_done.sem, count_b((PAIRS - 1, k // 4), 1))
                raw = w_raw[:, k % 2].rearrange("p (a n) -> p a n", a=2)
                nc.gpsimd.tensor_scalar(wo_rows[k][:, 0], raw, 1.0, None, ALU.mult).then_inc(wo_high, 1)
                pool.wait_ge(wo_high, k + 1)
                nc.gpsimd.tensor_tensor(wo_rows[k][:, 1], raw, wo_rows[k][:, 0], ALU.subtract).then_inc(wo_split, 1)
            pool.wait_ge(gb_in, 32)
            with pool.Fori(0, NT // 2) as t2:
                for i in range(2):
                    pool.wait_ge(normed, t2 * 2 + (i + 1))
                    nc.gpsimd.tensor_tensor(res[i], res[i], gain, ALU.mult).then_inc(scaled, 1)
                    pool.wait_ge(scaled, t2 * 2 + (i + 1))
                    nc.gpsimd.tensor_tensor(res[i], res[i], shift, ALU.add).then_inc(shifted, 1)

        @block.tensor
        def _(pe):
            def project_first(c):
                pe.wait_ge(w_ready, c + 1)
                if c >= 2:
                    pe.wait_ge(raw_copied.sem, c - 1)
                for k2 in range(4):
                    pe.wait_ge(x_split, k2 + 1)
                    ins = dense(c, 0, range(6 * k2, 6 * k2 + 6))
                ins.then_inc(dense_done.sem, 1)

            project_first(0)
            project_first(1)
            pe.wait_ge(const_ready, 4)
            for sbn in range(SBS):
                pe.wait_ge(x_split, 4 * (sbn + 1))
                for n in range(24):
                    k, part = divmod(n, 3)
                    wp, xp = SPLIT_PARTS[part]
                    last = nc.tensor.matmul(bank[2 + sbn][0:2 * AH], ba_w[:, wp, k, :],
                                            xr[:, xp, k, sbn * UNIT:(sbn + 1) * UNIT], start=(n == 0), stop=(n == 23))
                last.then_inc(ba_projected, 1)
            project_first(2)
            for i in range(NT):
                pe.wait_ge(ba_copied, i // CH + 1)
                last = nc.tensor.transpose(bank[6][:, i * 8:(i + 1) * 8], ba_ch[:, i * P:(i + 1) * P],
                                           ident[0:2 * AH, 0:2 * AH])
            last.then_inc(ba_done, 1)
            project_first(3)
            pe.wait_ge(g_ready, 1)
            g_cols = pre[:, 5].rearrange("p h t -> p (h t)")
            nc.tensor.matmul(bank[3][:, 0:AH * NT], tri[:], g_cols, start=True, stop=True).then_inc(g_sums, 1)
            nc.tensor.matmul(bank[4][:, 0:AH * NT], ones[:], g_cols, start=True, stop=True).then_inc(g_sums, 1)
            pe.wait_ge(g_copied, 1)
            nc.tensor.transpose(bank[5][0:AH * NT, 0:P], pre[:, 2].rearrange("p h t -> p (h t)"), ident[:])\
                .then_inc(g_turn_done, 1)
            pe.wait_ge(g_turned_ready, 1)

            def turn_o(unit):
                pe.wait_ge(o_scaled_ready.sem, o_scaled_ready.at(unit, 1))
                for i in range(CH):
                    ins = nc.tensor.transpose(bank[6][:, i * P:(i + 1) * P], o_scaled[:, i], ident[:])
                ins.then_inc(ot_done.sem, 1)

            def slot_program(h, s):
                me = (h, s)
                nxt = next_slot(me)
                sbn = (s + 1) % SBS
                par = s % 2
                done = [0, 0, 0, 0]

                def fill(c, n):
                    a = done[c]
                    if a == 0:
                        if sbn == 0:
                            pe.wait_ge(w_ready, h * 4 + (4 + c + 1))
                        if c >= 2:
                            pe.wait_ge(raw_copied.sem, raw_copied.at(nxt, c - 1))
                        else:
                            pe.wait_ge(raw_copied.sem, raw_copied.at(me, c + 3))
                    ins = dense(c, sbn, range(a, a + n))
                    done[c] = a + n
                    if done[c] == 24:
                        ins.then_inc(dense_done.sem, 1)

                pe.wait_ge(prep_ready.sem, prep_ready.at(me, 1))
                if s > 0:
                    pe.wait_ge(o_ready.sem, o_ready.at(me, 0))
                    pe.wait_ge(state_ready.sem, state_ready.at(me, 0))
                for i in range(CH):
                    ins = nc.tensor.transpose(bank[5][:, i * P:(i + 1) * P], kq[:, par, 0, i * P:(i + 1) * P], ident[:])
                ins.then_inc(ktok_done.sem, 1)
                for i in range(CH):
                    ins = nc.tensor.transpose(bank[7][:, i * P:(i + 1) * P], kq[:, par, 1, i * P:(i + 1) * P], ident[:])
                ins.then_inc(qtok_done.sem, 1)
                for hf in range(2):
                    for i in range(2):
                        t = 2 * hf + i
                        ins = nc.tensor.matmul(half_bank[hf][:, i * 256:(i + 1) * 256],
                                               kq[:, par, 0, t * P:(t + 1) * P], kq[:, par, :, t * P:(t + 1) * P],
                                               start=True, stop=True)
                    ins.then_inc(kk_done.sem, 1)
                    if hf == 0 and s > 0:
                        turn_o((h, s - 1))
                fill(0, START_FILL[0])
                pe.wait_ge(prep_ready.sem, prep_ready.at(me, 2))
                pe.wait_ge(y_out_ready.sem, y_out_ready.at(me, 0))
                for i in range(CH):
                    ins = nc.tensor.transpose(bank[6][:, i * P:(i + 1) * P], v_ch[:, i * P:(i + 1) * P], ident[:])
                ins.then_inc(vtok_done.sem, 1)
                fill(0, START_FILL[1])
                for hf in range(2):
                    pe.wait_ge(zp_ready.sem, zp_ready.at(me, 2 * hf + 2))
                    for i in range(2):
                        ins = nc.tensor.transpose(half_bank[hf][:, i * P:(i + 1) * P], p_buf[:, 2 * hf + i], ident[:])
                    ins.then_inc(zt_done.sem, 1)
                fill(0, START_FILL[2])
                for hf in range(2):
                    pe.wait_ge(t1_ready.sem, t1_ready.at(me, hf + 1))
                    for i in range(2):
                        ins = nc.tensor.transpose(half_bank[hf][:, i * P:(i + 1) * P], t_inv[:, 2 * hf + i], ident[:])
                    ins.then_inc(y1_done.sem, 1)
                fill(0, START_FILL[3])
                for l in range(LEVELS):
                    for hf in range(2):
                        if l == 0:
                            pe.wait_ge(y1_copied.sem, y1_copied.at(me, hf + 1))
                        else:
                            pe.wait_ge(y_ready.sem, y_ready.at(me, 2 * (l - 1) + hf + 1))
                        for i in range(2):
                            t = 2 * hf + i
                            ins = nc.tensor.matmul(half_bank[hf][:, i * P:(i + 1) * P], n_buf[:, t], y_inv[:, t],
                                                   start=True, stop=True)
                        ins.then_inc(p_done.sem, 1)
                        if l > 0:
                            if l == 1:
                                pe.wait_ge(k_dec_ready.sem, k_dec_ready.at(me, 1))
                            for i in range(2):
                                ins = nc.tensor.transpose(turn_bank[hf][:, i * P:(i + 1) * P],
                                                          y_inv[:, 2 * hf + i], ident[:])
                            ins.then_inc(turn_done.sem, 1)
                    for c, n in LEVEL_FILL[2 * l]:
                        fill(c, n)
                    for hf in range(2):
                        pe.wait_ge(p_copied.sem, p_copied.at(me, 2 * l + hf + 1))
                        if l > 0:
                            pe.wait_ge(t_copied.sem, t_copied.at(me, 2 * (l - 1) + hf + 1))
                        for i in range(2):
                            t = 2 * hf + i
                            ins = nc.tensor.matmul(half_bank[hf][:, i * P:(i + 1) * P], t_inv[:, t], p_buf[:, t],
                                                   start=True, stop=True)
                        ins.then_inc(yy_done.sem, 1)
                    for c, n in LEVEL_FILL[2 * l + 1]:
                        fill(c, n)
                for i in range(CH):
                    if i == 0:
                        pe.wait_ge(beta_v_ready.sem, beta_v_ready.at(me, 1))
                        if s == 0:
                            pe.wait_ge(state_zeroed, h + 1)
                    pe.wait_ge(state_ready.sem, state_ready.at(me, i))
                    nc.tensor.matmul(bank[5][:, 0:P], kq[:, par, 0, i * P:(i + 1) * P], state[:],
                                     start=True, stop=True).then_inc(ks_done.sem, 1)
                    nc.tensor.matmul(bank[6][:, 0:P], kq[:, par, 1, i * P:(i + 1) * P], state[:],
                                     start=True, stop=True).then_inc(qs_done.sem, 1)
                    for c, n in STEP_FILL[i][0]:
                        fill(c, n)
                    if i == 0:
                        pe.wait_ge(y_ready.sem, y_ready.at(me, 2 * LEVELS))
                    pe.wait_ge(resid_ready.sem, resid_ready.at(me, i + 1))
                    nc.tensor.matmul(bank[5][:, 0:P], y_inv[:, i], resid[:], start=True, stop=True)\
                        .then_inc(tr_done.sem, 1)
                    for c, n in STEP_FILL[i][1]:
                        fill(c, n)
                    pe.wait_ge(v_new_ready.sem, v_new_ready.at(me, i + 1))
                    nc.tensor.matmul(bank[5][:, 0:P], k_dec[:, i], v_new[:], start=True, stop=True)\
                        .then_inc(kv_done.sem, 1)
                    nc.tensor.matmul(bank[7][:, 0:P], pt[:, i], v_new[:], start=True, stop=True)\
                        .then_inc(o_done.sem, 1)
                    for c, n in STEP_FILL[i][2]:
                        fill(c, n)
                fill(3, END_FILL)
                assert done == [24] * 4, done
                if s == SBS - 1:
                    turn_o(me)

            with pe.Fori(0, AH) as h:
                for s in range(SBS):
                    slot_program(h, s)

            def attention_unit(j, s):
                me = (j, s)
                nxt, kinds = next_tiles(j, s)
                todo = 24 * len(kinds)
                sbn = (s + 1) % SBS
                done = [0]

                def fill(n):
                    for _ in range(min(n, todo - done[0])):
                        c, step = divmod(done[0], 24)
                        if step == 0:
                            if sbn == 0:
                                pe.wait_ge(w_ready, j * 2 + (21 + c))
                            pe.wait_ge(raw_copied.sem, count_b(nxt, c) - 2)
                        ins = dense(c, sbn, [step], place=kinds[c][0])
                        done[0] += 1
                        if step == 23:
                            ins.then_inc(dense_done.sem, 1)

                first = type(j) is int and j == 0 and s == 0

                def scores(i):
                    qt = s * CH + i
                    k0 = max(qt - 1, 0) * P
                    n = (qt + 1) * P - k0
                    for hd in range(2):
                        rows = slice(hd * BD, (hd + 1) * BD)
                        if i >= 2:
                            pe.wait_ge(max_ready.sem, max_ready.at(me, 2 * (i - 2) + hd + 1))
                        nc.tensor.matmul(bank[2 + 2 * (i % 2) + hd][:, 0:n], q_in[s % 2][rows, i * P:(i + 1) * P],
                                         k_ch[rows, k0:k0 + n], start=True, stop=True).then_inc(score_done.sem, 1)

                def turn(i):
                    pe.wait_ge(p_scaled.sem, p_scaled.at(me, 2 * i + 2))
                    if i > 0:
                        pe.wait_ge(p_turned_ready.sem, p_turned_ready.at(me, i))
                    for hd in range(2):
                        for kb in range(1 if (s, i) == (0, 0) else 2):
                            q = 2 * hd + kb
                            ins = nc.tensor.transpose(bank[6][:, q * P:(q + 1) * P],
                                                      score[:, i % 2, hd, kb * P:(kb + 1) * P], ident[:])
                    ins.then_inc(p_turn_done.sem, 1)

                def values(i):
                    qt = s * CH + i
                    kbs = [0] if qt == 0 else [0, 1]
                    pe.wait_ge(p_turned_ready.sem, p_turned_ready.at(me, i + 1))
                    for hd in range(2):
                        for kb in kbs:
                            ins = nc.tensor.matmul(bank[7][hd * BD:(hd + 1) * BD, i * P:(i + 1) * P],
                                                   v_tok[:, max(qt - 1, 0) + kb, hd * BD:(hd + 1) * BD],
                                                   p_turned[i % 2][:, 2 * hd + kb],
                                                   start=(kb == kbs[0]), stop=(kb == kbs[-1]))
                    ins.then_inc(pv_done.sem, 1)

                if type(j) is int and j == 0 and s == 0:
                    pe.wait_ge(moved, 4)
                else:
                    pe.wait_ge(raw_copied.sem, count_b(me, 2 if (type(j) is int and j == 0) else 0))
                if not first:
                    pe.wait_ge(max_ready.sem, max_ready.at(me, 0))
                    pe.wait_ge(p_turned_ready.sem, p_turned_ready.at(me, 0))
                if type(j) is int and j == 0:
                    for i in range(CH):
                        ins = nc.tensor.transpose(bank[6][:, i * P:(i + 1) * P], v_ch[:, i * P:(i + 1) * P], ident[:])
                    ins.then_inc(vt_done.sem, 1)
                scores(0)
                scores(1)
                f = todo // 24 * 3
                fill(2 * f)
                if type(j) is int and j == 0:
                    pe.wait_ge(vt_copied.sem, s + 1)
                turn(0)
                scores(2)
                fill(f)
                if not first:
                    pe.wait_ge(y_b_ready.sem, y_b_ready.at(me, 0))
                values(0)
                turn(1)
                scores(3)
                fill(f)
                values(1)
                turn(2)
                fill(f)
                values(2)
                turn(3)
                fill(f)
                values(3)
                fill(96)

            attention_units(pe, attention_unit)

            pe.wait_ge(wo_split, KT)
            def project_tiles(t2, first):
                for i in range(2):
                    pe.wait_ge(y_low, t2 * 2 + (i + 1))
                    for half in range(2):
                        if not first:
                            pe.wait_ge(res_ready, t2 * 4 + (2 * i + half - 3))
                        for n in range(3 * KT):
                            k, part = divmod(n, 3)
                            wp, yp = SPLIT_PARTS[part]
                            ins = nc.tensor.matmul(bank[2 * i + half][:], y_split[i][:, yp, k],
                                                   wo_rows[k][:, wp, half],
                                                   start=(n == 0), stop=(n == 3 * KT - 1))
                        ins.then_inc(proj_done, 1)

            project_tiles(0, True)
            with pe.Fori(1, NT // 2) as t2:
                project_tiles(t2, False)

        @block.scalar
        def _(act):
            for dst, src in ((ident[:], c_ident), (tri[:], c_tri), (ba_raw[:], w_ba), (masks_raw, c_masks),
                             (convw_all[:, 0:AH], conv_w), (normw[:], norm_w),
                             (dtb[:], dt_bias), (alog[:], a_log),
                             (pair_all[:, :, SLOPE], c_slope), (pair_all[:, :, SINK], sinks)):
                act.dma_start(dst, src).then_inc(const_in, 16)
            act.preload_act_table_set(EXP_LN_SET)
            def x_high_part(n):
                sbn, k2 = divmod(n, 4)
                act.wait_ge(x_in[n % 4], 16 * (n // 4 + 1))
                nc.scalar.activation(xr[:, 0, 2 * k2:2 * k2 + 2, sbn * UNIT:(sbn + 1) * UNIT], x_stage[n % 4], ACT.Copy)\
                    .then_inc(x_high, 1)

            def copy_raw(unit, c):
                act.wait_ge(dense_done.sem, dense_done.at(unit, c + 1))
                dst = conv_in[:, c, CONV - 1:] if c < 3 else z_raw[:]
                nc.scalar.activation(dst, dense_bank[c % 2][:], ACT.Copy).then_inc(raw_copied.sem, 1)

            for n in range(8):
                x_high_part(n)
            copy_raw((0, 0), 0)
            for n in range(8, 10):
                x_high_part(n)
            copy_raw((0, 0), 1)
            for n in range(10, 16):
                x_high_part(n)
            copy_raw((0, 0), 2)
            act.wait_ge(const_in, 16 * N_CONST)
            nc.scalar.activation(ea[:], alog[:], ACT.Exp).then_inc(pre_act, 1)
            act.wait_ge(pre_dve, 4)
            nc.scalar.activation(pre[:, 2], pre[:, 1], ACT.Exp, scale=-1.0).then_inc(pre_act, 1)
            nc.scalar.activation(pre[:, 3], pre[:, 6], ACT.Exp, scale=-1.0).then_inc(pre_act, 1)
            act.wait_ge(pre_act, 2)
            nc.scalar.activation(pre[:, 4], pre[:, 2], ACT.Ln, bias=1.0).then_inc(pre_act, 1)
            copy_raw((0, 0), 3)
            act.wait_ge(g_diff, 2)
            nc.scalar.activation(cols_all[:, :, EG], cols_all[:, :, G_], ACT.Exp).then_inc(pre_act, 1)
            nc.scalar.activation(cols_all[:, :, EKD], pre[:, 4], ACT.Exp).then_inc(pre_act, 1)
            nc.scalar.activation(cols_all[:, :, EGT], bank[4][:, 0:AH * NT].rearrange("p (h t) -> p h t", h=AH),
                                 ACT.Exp).then_inc(pre_act, 1)

            def prepare(unit, s):
                kq_s = kq[:, s % 2].rearrange("p a n -> p (a n)")
                act.wait_ge(conv_ready.sem, conv_ready.at(unit, 2))
                nc.scalar.activation(kq_s, kq_s, ACT.Silu).then_inc(prep_ready.sem, 1)
                act.wait_ge(conv_ready.sem, conv_ready.at(unit, 3))
                nc.scalar.activation(v_ch[:], v_ch[:], ACT.Silu).then_inc(prep_ready.sem, 1)

            def load_g_row(unit, row):
                rows = g_rows[bass.ds(row, CH)].rearrange("t n -> (t n)")
                act.dma_start(decay.rearrange("p t n -> p (t n)"), rows.partition_broadcast(P)).then_inc(g_row_in.sem, 16)

            prepare((0, 0), 0)
            act.wait_ge(g_stored, 32)
            load_g_row((0, 0), 0)

            def slot_program(h, s):
                me = (h, s)
                nxt = next_slot(me)
                if s == 0:
                    act.preload_act_table_set(EXP_LN_SET)
                def squares(a, turned, src, dst):
                    act.wait_ge(turned.sem, turned.at(me, 1))
                    for i in range(CH):
                        nc.scalar.activation(dst[:, i], src[:, i * P:(i + 1) * P], ACT.Square,
                                             accum_out=sums_sq[:, a, i:i + 1]).then_inc(kq_ss_ready.sem, 1)

                squares(0, ktok_done, bank[5], n_buf)
                act.wait_ge(kq_ss_ready.sem, kq_ss_ready.at(me, CH))
                nc.scalar.activation(ln_ss[:, 0], sums_sq[:, 0], ACT.Ln, bias=eps[:, 0:1]).then_inc(ln_ready.sem, 1)
                act.wait_ge(ln_ready.sem, ln_ready.at(me, 1))
                nc.scalar.activation(r_k[:], ln_ss[:, 0], ACT.Exp, scale=-0.5).then_inc(rk_ready.sem, 1)
                squares(1, qtok_done, bank[7], p_buf)
                act.wait_ge(gdiff_ready.sem, gdiff_ready.at(me, CH))
                nc.scalar.activation(decay, decay, ACT.Exp).then_inc(decay_ready.sem, 1)
                act.wait_ge(kq_ss_ready.sem, kq_ss_ready.at(me, 2 * CH))
                nc.scalar.activation(ln_ss[:, 1], sums_sq[:, 1], ACT.Ln, bias=eps[:, 0:1]).then_inc(ln_ready.sem, 1)
                act.wait_ge(ln_ready.sem, ln_ready.at(me, 2))
                nc.scalar.activation(rq2[:], ln_ss[:, 1], ACT.Exp, scale=-1.0).then_inc(rk_ready.sem, 1)
                for hf in range(2):
                    act.wait_ge(y1_done.sem, y1_done.at(me, hf + 1))
                    nc.scalar.activation(halves(y_inv)[hf], tiles(half_bank[hf], 2), ACT.Copy)\
                        .then_inc(y1_copied.sem, 1)
                act.wait_ge(zp_ready.sem, zp_ready.at(me, 4))
                load_g_row(nxt, h * NT + (s + 1) * CH)
                for l in range(LEVELS):
                    for hf in range(2):
                        act.wait_ge(p_done.sem, p_done.at(me, 2 * l + hf + 1))
                        nc.scalar.activation(halves(p_buf)[hf], tiles(half_bank[hf], 2), ACT.Copy)\
                            .then_inc(p_copied.sem, 1)
                        if l > 0:
                            act.wait_ge(turn_done.sem, turn_done.at(me, 2 * (l - 1) + hf + 1))
                            nc.scalar.activation(halves(t_inv)[hf], tiles(turn_bank[hf], 2), ACT.Copy)\
                                .then_inc(t_copied.sem, 1)
                    if l in RAW_COPY_AT:
                        c = RAW_COPY_AT.index(l)
                        act.wait_ge(tail_saved.sem, tail_saved.at(me, c + 1))
                        copy_raw(nxt, c)
                act.wait_ge(y_out_ready.sem, y_out_ready.at(me, 0))
                act.wait_ge(raw_copied.sem, raw_copied.at(me, 4))
                nc.scalar.activation(gate[:], z_raw[:], ACT.Silu).then_inc(gate_ready.sem, 1)
                act.wait_ge(y_ready.sem, y_ready.at(me, 2 * LEVELS))
                prepare(nxt, s + 1)
                act.preload_act_table_set(EXP_LN_SET)
                act.wait_ge(small.sem, small.at(me, 5))
                nc.scalar.activation(rms_ln[:], rms_in[:], ACT.Ln, bias=eps[:, 0:1]).then_inc(rms_ln_ready.sem, 1)
                act.wait_ge(small.sem, small.at(me, 6))
                nc.scalar.activation(o_scale[:], rms_sum[:], ACT.Exp, scale=-0.5).then_inc(o_scale_ready.sem, 1)
                copy_raw(nxt, 3)

            with act.Fori(0, AH) as h:
                for s in range(SBS):
                    slot_program(h, s)

            act.wait_ge(y_out_ready.sem, y_out_ready.at((AH, 0), 0))
            act.wait_ge(prep_ready.sem, prep_ready.at((AH, 0), 2))
            act.wait_ge(raw_copied.sem, raw_copied.at((AH, 0), 4))
            act.wait_ge(g_row_in.sem, g_row_in.at((AH, 0), 16))
            act.wait_ge(tail_saved.sem, 3 * (SBS * AH + 1))
            nc.scalar.activation(k_ch[:, 0:UNIT], conv_in[:, 0, CONV - 1:], ACT.Copy).then_inc(moved, 1)
            nc.scalar.activation(v_ch[:], conv_in[:, 1, CONV - 1:], ACT.Copy).then_inc(moved, 1)
            nc.scalar.activation(q_in[0], conv_in[:, 2, CONV - 1:], ACT.Copy).then_inc(moved, 1)
            nc.scalar.activation(z_in[0], z_raw[:], ACT.Copy).then_inc(moved, 1)

            def attention_unit(j, s):
                me = (j, s)
                nxt, kinds = next_tiles(j, s)
                sn = (s + 1) % SBS

                def copy_next(c):
                    act.wait_ge(dense_done.sem, count_b(nxt, c))
                    kind = kinds[c][1]
                    if kind == "v":
                        act.wait_ge(vt_done.sem, s + 1)
                    dst = {"k": k_ch[:, sn * UNIT:(sn + 1) * UNIT], "v": v_ch[:], "q": q_in[sn % 2], "z": z_in[sn % 2]}[kind]
                    nc.scalar.activation(dst, dense_bank[c % 2][:], ACT.Copy).then_inc(raw_copied.sem, 1)

                for i in range(CH):
                    keys = slice(0, n_keys(j, s, i))
                    act.wait_ge(nmax_ready.sem, nmax_ready.at(me, i + 1))
                    for hd in range(2):
                        sc = score[:, i % 2, hd, keys]
                        nc.scalar.activation(sc, sc, ACT.Exp, bias=neg_max[:, i, hd:hd + 1],
                                             accum_out=row_sum[:, i, hd:hd + 1]).then_inc(exp_ready.sem, 1)
                    act.wait_ge(sink_in_ready.sem, sink_in_ready.at(me, i + 1))
                    nc.scalar.activation(sink_exp[:, i], sink_in[:, i], ACT.Exp).then_inc(sink_exp_ready.sem, 1)
                    if i == CH - 1:
                        if type(j) is int and j == 0 and s == 0:
                            act.wait_ge(moved, 4)
                        else:
                            act.wait_ge(raw_copied.sem, count_b(me, 3 if (type(j) is int and j == 0) else 1))
                            act.wait_ge(y_b_ready.sem, y_b_ready.at(me, 0))
                        nc.scalar.activation(gate[:], z_in[s % 2], ACT.Silu).then_inc(gate_b_ready.sem, 1)
                        act.preload_act_table_set(EXP_LN_SET)
                    for c in COPY_AT[len(kinds)][i]:
                        copy_next(c)

            attention_units(act, attention_unit)

            def high(t2, i):
                act.wait_ge(y_in[i], t2 * 16 + 16)
                nc.scalar.activation(y_split[i][:, 0], y_tile[i], ACT.Copy).then_inc(y_high, 1)

            def inverse_deviation(t2, i):
                act.wait_ge(moments_ready, t2 * 2 + (i + 1))
                nc.scalar.activation(ln_var[:], moments[:, 1:2], ACT.Ln, bias=eps[:, 1:2]).then_inc(var_ready, 1)
                act.wait_ge(var_ready, t2 * 2 + (i + 1))
                nc.scalar.activation(rstd[:], ln_var[:], ACT.Exp, scale=-0.5).then_inc(rstd_ready, 1)

            high(0, 0)
            high(0, 1)
            with act.Fori(0, NT // 2 - 1) as t2:
                act.preload_act_table_set(EXP_LN_SET)
                for i in range(2):
                    inverse_deviation(t2, i)
                    act.wait_ge(proj_done, t2 * 4 + (2 * i + 2))
                    high(t2 + 1, i)
            for i in range(2):
                inverse_deviation(NT // 2 - 1, i)

        @block.vector
        def _(dve):
            def x_low_part(n):
                sbn, k2 = divmod(n, 4)
                at = (slice(2 * k2, 2 * k2 + 2), slice(sbn * UNIT, (sbn + 1) * UNIT))
                dve.wait_ge(x_high, n + 1)
                nc.vector.tensor_tensor(xr[:, 1, at[0], at[1]], x_stage[n % 4], xr[:, 0, at[0], at[1]], ALU.subtract)\
                    .then_inc(x_split, 1)

            nc.vector.memset(ones[:], 1.0).then_inc(const_ready, 1)
            nc.vector.memset(eps[:, 0:1], L2_EPS)
            nc.vector.memset(eps[:, 1:2], LN_EPS)
            nc.vector.memset(convw_all[:, AH:AH + 1], 0.0)
            nc.vector.memset(conv_in[:, :, 0:CONV - 1], 0.0).then_inc(pre_dve, 1)
            for n in range(4):
                x_low_part(n)
            dve.wait_ge(const_in, 16 * N_CONST)
            nc.vector.tensor_copy(masks[:].rearrange("p a n -> p (a n)"), masks_raw).then_inc(masks_ready, 1)
            nc.vector.tensor_scalar(closed[:], tri[:], -1.0, -MASKED, ALU.add, ALU.mult).then_inc(const_ready, 1)
            nc.vector.tensor_copy(ba_w[:, 0], ba_raw[:]).then_inc(const_ready, 1)
            dve.wait_ge(const_ready, 3)
            nc.vector.tensor_tensor(ba_w[:, 1], ba_raw[:], ba_w[:, 0], ALU.subtract).then_inc(const_ready, 1)
            nc.vector.tensor_scalar(normw[:], normw[:], float(P) ** -0.5, None, ALU.mult).then_inc(const_ready, 1)
            nc.vector.tensor_copy(convw[:], convw_all[:, 0]).then_inc(convw_staged, 1)
            nc.vector.tensor_scalar(pair_all[:, :, NSINK], pair_all[:, :, SINK], -1.0, None, ALU.mult)\
                .then_inc(pre_dve, 1)
            for n in range(4, 16):
                x_low_part(n)

            def conv(unit, s, c, step, part=(0, UNIT), piece=None):
                last = CONV - 1 if piece is None else 2 * CONV - 1
                piece = step if piece is None else piece
                acc = (kq[:, s % 2, 1], kq[:, s % 2, 0], v_ch)[c][:, part[0]:part[1]]
                tap = conv_in[:, c, step + part[0]:step + part[1]]
                if piece == 0:
                    dve.wait_ge(raw_copied.sem, raw_copied.at(unit, c + 1))
                if step == 0:
                    nc.vector.tensor_scalar(acc, tap, convw[:, c, 0:1], None, ALU.mult).then_inc(conv_step.sem, 1)
                    return
                dve.wait_ge(conv_step.sem, conv_step.at(unit, 3 * c + piece))
                ins = nc.vector.scalar_tensor_tensor(acc, tap, convw[:, c, step:step + 1], acc, ALU.mult, ALU.add)
                if piece < last:
                    ins.then_inc(conv_step.sem, 1)
                    return
                ins.then_inc(conv_ready.sem, 1)
                if s == SBS - 1:
                    ins = nc.vector.memset(conv_in[:, c, 0:CONV - 1], 0.0)
                else:
                    ins = nc.vector.tensor_copy(conv_in[:, c, 0:CONV - 1], conv_in[:, c, UNIT:UNIT + CONV - 1])
                ins.then_inc(tail_saved.sem, 1)

            def conv_v(unit, s, piece):
                step, half = divmod(piece, 2)
                conv(unit, s, 2, step, (half * UNIT // 2, (half + 1) * UNIT // 2), piece)

            dve.wait_ge(convw_staged, 1)
            for c in range(2):
                for step in range(CONV):
                    conv((0, 0), 0, c, step)

            for i in range(SBS):
                dve.wait_ge(ba_projected, i + 1)
                nc.vector.tensor_copy(ba_ch[:, i * UNIT:(i + 1) * UNIT], bank[2 + i][0:2 * AH]).then_inc(ba_copied, 1)
            ba = bank[6][:, 0:NT * 2 * AH].rearrange("p (t c h) -> p c h t", c=2, h=AH)
            heads = [P, AH, NT]
            dve.wait_ge(ba_done, 1)
            nc.vector.tensor_tensor(pre[:, 0], ba[:, 1], dtb[:].unsqueeze(2).to_broadcast(heads), ALU.add)\
                .then_inc(pre_dve, 1)
            nc.vector.tensor_copy(pre[:, 6], ba[:, 0])
            dve.wait_ge(pre_dve, 3)
            nc.vector.scalar_tensor_tensor(pre[:, 1], pre[:, 0], -1.0, pre[:, 0], ALU.mult, ALU.max)\
                .then_inc(pre_dve, 1)
            dve.wait_ge(pre_act, 4)
            nc.vector.tensor_scalar(pre[:, 3], pre[:, 3], 1.0, None, ALU.add).then_inc(pre_dve, 1)
            nc.vector.scalar_tensor_tensor(pre[:, 1], pre[:, 0], 0.0, pre[:, 4], ALU.max, ALU.add)\
                .then_inc(pre_dve, 1)
            dve.wait_ge(pre_dve, 5)
            nc.vector.reciprocal(cols_all[:, :, BETA], pre[:, 3]).then_inc(pre_dve, 1)
            dve.wait_ge(pre_dve, 6)
            nc.vector.scalar_tensor_tensor(pre[:, 5], pre[:, 1], -1.0, ea[:].unsqueeze(2).to_broadcast(heads),
                                           ALU.mult, ALU.mult).then_inc(g_ready, 1)
            dve.wait_ge(pre_dve, 7)
            nc.vector.tensor_scalar(cols_all[:, :, NBETA], cols_all[:, :, BETA], -1.0, None, ALU.mult)\
                .then_inc(pre_dve, 1)
            for piece in range(2 * CONV):
                conv_v((0, 0), 0, piece)
            dve.wait_ge(g_ready, 1)
            dve.wait_ge(g_sums, 2)
            nc.vector.tensor_copy(pre[:, 2], bank[3][:, 0:AH * NT].rearrange("p (h t) -> p h t", h=AH))\
                .then_inc(g_copied, 1)
            nc.vector.tensor_copy(cols_all[:, :, G_], bank[3][:, 0:AH * NT].rearrange("p (h t) -> p h t", h=AH))\
                .then_inc(g_diff, 1)
            dve.wait_ge(g_diff, 1)
            nc.vector.tensor_tensor(pre[:, 4], bank[4][:, 0:AH * NT].rearrange("p (h t) -> p h t", h=AH),
                                    cols_all[:, :, G_], ALU.subtract).then_inc(g_diff, 1)
            dve.wait_ge(g_turn_done, 1)
            nc.vector.tensor_copy(g_turned, bank[5][0:AH * NT, 0:P]).then_inc(g_turned_ready, 1)
            dve.wait_ge(masks_ready, 1)
            dve.wait_ge(pre_act, 7)
            dve.wait_ge(pre_dve, 8)

            def gated(unit, s):
                h = unit[0]
                dve.wait_ge(ot_done.sem, ot_done.at(unit, 1))
                dve.wait_ge(gate_ready.sem, gate_ready.at(unit, 1))
                dve.wait_ge(y_spilled[s % 2], h * 32 + (16 * (s // 2) + 1))
                nc.vector.scalar_tensor_tensor(y_out[:, s % 2], bank[6][:], normw[:], gate[:], ALU.mult, ALU.mult)\
                    .then_inc(y_out_ready.sem, 1)

            def slot_program(h, s):
                me = (h, s)
                nxt = next_slot(me)
                of_unit = slice(s * CH, (s + 1) * CH)

                def next_conv(c, step):
                    conv(nxt, (s + 1) % SBS, c, step)

                v_pieces = iter(range(2 * CONV))

                def next_v_pieces(n):
                    for _ in range(n):
                        conv_v(nxt, (s + 1) % SBS, next(v_pieces))

                if s == 0:
                    nc.vector.tensor_copy(cols[:], cols_all[:, bass.ds(h, 1)].rearrange("p a c t -> p (a c) t"))\
                        .then_inc(cols_staged, 1)
                    nc.vector.memset(state[:], 0.0).then_inc(state_zeroed, 1)
                    dve.wait_ge(cols_staged, h + 1)
                if s == SBS - 1:
                    nc.vector.tensor_copy(convw[:], convw_all[:, bass.ds(h + 1, 1)].rearrange("p a c t -> p (a c) t"))\
                        .then_inc(convw_staged, 1)
                if s > 0:
                    gated((h, s - 1), s - 1)
                dve.wait_ge(ln_ready.sem, ln_ready.at(me, 1))
                nc.vector.scalar_tensor_tensor(col_s[:], ln_ss[:, 0], 0.5, cols[:, G_, of_unit], ALU.mult, ALU.add)\
                    .then_inc(small.sem, 1)
                dve.wait_ge(small.sem, small.at(me, 1))
                dve.wait_ge(g_row_in.sem, g_row_in.at(me, 16))
                for i in range(CH):
                    nc.vector.scalar_tensor_tensor(decay[:, i], decay[:, i], col_s[:, i:i + 1], closed[:],
                                                   ALU.subtract, ALU.add).then_inc(gdiff_ready.sem, 1)
                dve.wait_ge(rk_ready.sem, rk_ready.at(me, 1))
                nc.vector.tensor_tensor(nb_rk[:], cols[:, NBETA, of_unit], r_k[:], ALU.mult).then_inc(small.sem, 1)
                nc.vector.tensor_tensor(kd_s[:], cols[:, EKD, of_unit], r_k[:], ALU.mult).then_inc(small.sem, 1)
                dve.wait_ge(small.sem, small.at(me, 3))
                nc.vector.tensor_tensor(w_ks[:], nb_rk[:], cols[:, EG, of_unit], ALU.mult).then_inc(small.sem, 1)
                dve.wait_ge(decay_ready.sem, decay_ready.at(me, 1))
                for hf in range(2):
                    both = half_bank[hf][:].rearrange("p (t a n) -> p t a n", t=2, a=2)
                    dve.wait_ge(kk_done.sem, kk_done.at(me, hf + 1))
                    nc.vector.tensor_tensor(halves(p_buf)[hf], both[:, :, 0], halves(decay)[hf], ALU.mult)\
                        .then_inc(zp_ready.sem, 1)
                    nc.vector.tensor_tensor(halves(pt)[hf], both[:, :, 1], halves(decay)[hf], ALU.mult)\
                        .then_inc(zp_ready.sem, 1)
                dve.wait_ge(ktok_done.sem, ktok_done.at(me, 1))
                nc.vector.tensor_tensor(k_dec, tiles(bank[5]), per_tile(kd_s[:]), ALU.mult)\
                    .then_inc(k_dec_ready.sem, 1)
                for hf in range(2):
                    dve.wait_ge(zt_done.sem, zt_done.at(me, hf + 1))
                    nc.vector.tensor_tensor(halves(n_buf)[hf], tiles(half_bank[hf], 2),
                                            per_tile(nb_rk[:, 2 * hf:2 * hf + 2], 2), ALU.mult).then_inc(n_ready.sem, 1)
                dve.wait_ge(t_cleared.sem, t_cleared.at(me, 1))
                for hf in range(2):
                    dve.wait_ge(n_ready.sem, n_ready.at(me, hf + 1))
                    settle(dve)
                    nc.vector.copy_predicated(halves(t_inv)[hf], first.unsqueeze(1).to_broadcast([P, 2, P]),
                                              halves(n_buf)[hf]).then_inc(t1_ready.sem, 1)
                dve.wait_ge(vtok_done.sem, vtok_done.at(me, 1))
                nc.vector.tensor_tensor(beta_v, tiles(bank[6]), per_tile(cols[:, BETA, of_unit]), ALU.mult)\
                    .then_inc(beta_v_ready.sem, 1)
                if s == SBS - 1:
                    dve.wait_ge(convw_staged, h + 2)
                for l in range(LEVELS):
                    for hf in range(2):
                        dve.wait_ge(yy_done.sem, yy_done.at(me, 2 * l + hf + 1))
                        settle(dve)
                        nc.vector.copy_predicated(halves(y_inv)[hf],
                                                  levels[:, l].unsqueeze(1).to_broadcast([P, 2, P]),
                                                  tiles(half_bank[hf], 2)).then_inc(y_ready.sem, 1)
                    for c, step in CONV_AT[l]:
                        next_conv(c, step)
                for i in range(CH):
                    one = slice(i, i + 1)
                    dve.wait_ge(ks_done.sem, ks_done.at(me, i + 1))
                    if i == 0:
                        dve.wait_ge(small.sem, small.at(me, 4))
                        dve.wait_ge(beta_v_ready.sem, beta_v_ready.at(me, 1))
                    nc.vector.scalar_tensor_tensor(resid[:], bank[5][:, 0:P], w_ks[:, one], beta_v[:, i],
                                                   ALU.mult, ALU.add).then_inc(resid_ready.sem, 1)
                    dve.wait_ge(qs_done.sem, qs_done.at(me, i + 1))
                    nc.vector.tensor_scalar(q_state[:], bank[6][:, 0:P], cols[:, EG, s * CH + i:s * CH + i + 1], None,
                                            ALU.mult).then_inc(q_state_ready.sem, 1)
                    next_v_pieces(V_CONV_AT[i][0])
                    dve.wait_ge(tr_done.sem, tr_done.at(me, i + 1))
                    nc.vector.tensor_copy(v_new[:], bank[5][:, 0:P]).then_inc(v_new_ready.sem, 1)
                    next_v_pieces(V_CONV_AT[i][1])
                    dve.wait_ge(kv_done.sem, kv_done.at(me, i + 1))
                    nc.vector.scalar_tensor_tensor(state[:], state[:], cols[:, EGT, s * CH + i:s * CH + i + 1],
                                                   bank[5][:, 0:P], ALU.mult, ALU.add).then_inc(state_ready.sem, 1)
                    dve.wait_ge(o_done.sem, o_done.at(me, i + 1))
                    dve.wait_ge(q_state_ready.sem, q_state_ready.at(me, i + 1))
                    nc.vector.tensor_tensor(o_tok[:, i], bank[7][:, 0:P], q_state[:], ALU.add).then_inc(o_ready.sem, 1)
                    dve.wait_ge(o_ready.sem, o_ready.at(me, i + 1))
                    nc.vector.tensor_tensor_reduce(out=o_scaled[:, i], in0=o_tok[:, i], in1=o_tok[:, i], scale=1.0,
                                                   scalar=0.0, op0=ALU.mult, op1=ALU.add, accum_out=ss_o[:, one])\
                        .then_inc(ss_ready.sem, 1)
                dve.wait_ge(ss_ready.sem, ss_ready.at(me, CH))
                dve.wait_ge(rk_ready.sem, rk_ready.at(me, 2))
                nc.vector.scalar_tensor_tensor(rms_in[:], ss_o[:], 1.0 / (P * P), rq2[:], ALU.mult, ALU.mult)\
                    .then_inc(small.sem, 1)
                dve.wait_ge(rms_ln_ready.sem, rms_ln_ready.at(me, 1))
                nc.vector.tensor_tensor(rms_sum[:], rms_ln[:], ln_ss[:, 1], ALU.add).then_inc(small.sem, 1)
                dve.wait_ge(o_scale_ready.sem, o_scale_ready.at(me, 1))
                nc.vector.tensor_tensor(o_scaled, o_tok, per_tile(o_scale[:]), ALU.mult).then_inc(o_scaled_ready.sem, 1)
                if s == SBS - 1:
                    gated(me, s)

            with dve.Fori(0, AH) as h:
                for s in range(SBS):
                    slot_program(h, s)

            def attention_unit(j, s):
                me = (j, s)
                if s == 0:
                    nc.vector.tensor_copy(pair[:], pair_all[:, bass.ds(j, 1)].rearrange("p a c h -> p (a c) h"))\
                        .then_inc(pair_staged, 1)
                    dve.wait_ge(pair_staged, j + 1)
                    for hd in range(2):
                        nc.vector.tensor_scalar(bias[:, hd], dist, pair[:, SLOPE, hd:hd + 1], None, ALU.mult)\
                            .then_inc(bias_ready, 1)
                    dve.wait_ge(bias_ready, j * 2 + 2)
                if type(j) is int and j == 0:
                    dve.wait_ge(vt_done.sem, s + 1)
                    nc.vector.tensor_copy(v_tok[:, s * CH:(s + 1) * CH], tiles(bank[6])).then_inc(vt_copied.sem, 1)

                def row_maxima(i):
                    n = n_keys(j, s, i)
                    if i >= 2:
                        dve.wait_ge(p_turn_done.sem, p_turn_done.at(me, i - 1))
                    for hd in range(2):
                        dve.wait_ge(score_done.sem, score_done.at(me, 2 * i + hd + 1))
                        settle(dve)
                        nc.vector.tensor_tensor_reduce(out=score[:, i % 2, hd, 0:n], in0=bank[2 + 2 * (i % 2) + hd][:, 0:n],
                                                       in1=bias[:, hd, 2 * P - n:], scale=BD ** -0.5, scalar=LOWEST,
                                                       op0=ALU.add, op1=ALU.max, accum_out=row_max[:, i, hd:hd + 1])\
                            .then_inc(max_ready.sem, 1)
                    dve.wait_ge(max_ready.sem, max_ready.at(me, 2 * i + 2))
                    nc.vector.scalar_tensor_tensor(neg_max[:, i], row_max[:, i], -1.0, pair[:, NSINK], ALU.mult, ALU.min)\
                        .then_inc(nmax_ready.sem, 1)
                    dve.wait_ge(nmax_ready.sem, nmax_ready.at(me, i + 1))
                    nc.vector.tensor_tensor(sink_in[:, i], neg_max[:, i], pair[:, SINK], ALU.add)\
                        .then_inc(sink_in_ready.sem, 1)

                def normalise_scores(i):
                    n = n_keys(j, s, i)
                    dve.wait_ge(exp_ready.sem, exp_ready.at(me, 2 * i + 2))
                    dve.wait_ge(sink_exp_ready.sem, sink_exp_ready.at(me, i + 1))
                    nc.vector.tensor_tensor(denom[:, i], row_sum[:, i], sink_exp[:, i], ALU.add).then_inc(denom_step.sem, 1)
                    dve.wait_ge(denom_step.sem, denom_step.at(me, 2 * i + 1))
                    nc.vector.reciprocal(denom_inv[:, i], denom[:, i]).then_inc(denom_step.sem, 1)
                    dve.wait_ge(denom_step.sem, denom_step.at(me, 2 * i + 2))
                    for hd in range(2):
                        p = score[:, i % 2, hd, 0:n]
                        nc.vector.tensor_scalar(p, p, denom_inv[:, i, hd:hd + 1], None, ALU.mult).then_inc(p_scaled.sem, 1)

                def copy_turned(i):
                    blocks = 1 if n_keys(j, s, i) == P else 2
                    view = lambda a: a.rearrange("p (h k) n -> p h k n", k=2)[:, :, 0:blocks]
                    dve.wait_ge(p_turn_done.sem, p_turn_done.at(me, i + 1))
                    if i >= 2:
                        dve.wait_ge(pv_done.sem, pv_done.at(me, i - 1))
                    nc.vector.tensor_copy(view(p_turned[i % 2]), view(tiles(bank[6]))).then_inc(p_turned_ready.sem, 1)

                row_maxima(0)
                row_maxima(1)
                normalise_scores(0)
                normalise_scores(1)
                copy_turned(0)
                row_maxima(2)
                copy_turned(1)
                normalise_scores(2)
                row_maxima(3)
                copy_turned(2)
                normalise_scores(3)
                copy_turned(3)
                dve.wait_ge(pv_done.sem, pv_done.at(me, CH))
                dve.wait_ge(gate_b_ready.sem, gate_b_ready.at(me, 1))
                dve.wait_ge(y_spilled[s % 2], j * 32 + (128 + 16 * (s // 2) + 1))
                nc.vector.tensor_tensor(y_out[:, s % 2], bank[7][:], gate[:], ALU.mult).then_inc(y_b_ready.sem, 1)

            dve.wait_ge(dist_in, 16)
            dve.wait_ge(moved, 4)
            attention_units(dve, attention_unit)

            def low(t2, i):
                dve.wait_ge(y_high, t2 * 2 + (i + 1))
                nc.vector.tensor_tensor(y_split[i][:, 1], y_tile[i], y_split[i][:, 0], ALU.subtract).then_inc(y_low, 1)

            def normalise(t2, i):
                dve.wait_ge(xt_in[i], t2 * 16 + 16)
                dve.wait_ge(out_sent[i], t2 * 16 + 1)
                for half in range(2):
                    part = slice(half * UNIT, (half + 1) * UNIT)
                    dve.wait_ge(proj_done, t2 * 4 + (2 * i + half + 1))
                    nc.vector.scalar_tensor_tensor(res[i][:, part], x_tile[i][:, part], ALPHA, bank[2 * i + half][:],
                                                   ALU.mult, ALU.add).then_inc(res_ready, 1)
                    dve.wait_ge(res_ready, t2 * 4 + (2 * i + half + 1))
                    nc.vector.bn_stats(stats[:, half], res[i][:, part]).then_inc(stats_ready, 1)
                dve.wait_ge(stats_ready, t2 * 4 + (2 * i + 2))
                settle(dve)
                nc.vector.bn_aggr(moments[:], stats[:].rearrange("p a c -> p (a c)")).then_inc(moments_ready, 1)
                dve.wait_ge(moments_ready, t2 * 2 + (i + 1))
                dve.wait_ge(rstd_ready, t2 * 2 + (i + 1))
                nc.vector.tensor_scalar(res[i], res[i], moments[:, 0:1], rstd[:], ALU.subtract, ALU.mult)\
                    .then_inc(normed, 1)

            low(0, 0)
            low(0, 1)
            with dve.Fori(0, NT // 2 - 1) as t2:
                for i in range(2):
                    normalise(t2, i)
                    low(t2 + 1, i)
            for i in range(2):
                normalise(NT // 2 - 1, i)


ORDER = ["xT", "x", "w_in", "w_ba", "conv_w", "a_log", "dt_bias", "norm_w", "sinks", "w_out", "ln_g", "ln_b",
         "c_tri", "c_ident", "c_masks", "c_dist", "c_slope"]


def layout(x, w_in, conv_w, a_log, dt_bias, norm_w, sinks, w_out, ln_g, ln_b):
    aw, bw, kvw = AH * P, 2 * PAIRS * BD, 2 * BD
    at = np.cumsum([0, aw, aw, aw, aw, AH, AH, bw, kvw, kvw, bw])
    qa, ka, va, za, ba, aa, qb, kb, vb, zb = at[:-1]
    wi = np.asarray(w_in)[0]
    cols = []
    for h in range(AH):
        for o in (qa, ka, va, za):
            cols.append(np.arange(o + h * P, o + (h + 1) * P))
    cols += [np.arange(kb, kb + P), np.arange(vb, vb + P)]
    pair = [np.concatenate([np.arange(j * BD, (j + 1) * BD), np.arange((PAIRS + j) * BD, (PAIRS + j + 1) * BD)])
            for j in range(PAIRS)]
    for j in range(PAIRS):
        cols += [qb + pair[j], zb + pair[j]]
    tiles = np.stack([wi[:, c].reshape(KT, P, P).transpose(1, 0, 2).reshape(P, KT * P) for c in cols])
    w_ba = wi[:, ba:ba + 2 * AH].reshape(KT, P, 2 * AH).transpose(1, 0, 2)
    cw = np.asarray(conv_w)[0].reshape(CONV, 3, AH, P).transpose(3, 2, 1, 0)
    rows = np.concatenate([np.arange(aw)] + [aw + p for p in pair])
    wo = np.asarray(w_out)[0][rows].reshape(KT, P, D)
    i = np.arange(P)
    r, c = i[:, None], i[None, :]
    levels = np.stack([((r // (2 * b) == c // (2 * b)) & (r // b % 2 == 0) & (c // b % 2 == 1))
                       for b in (2 << l for l in range(LEVELS))], 1)
    first = (r == c + 1) & (r % 2 == 1)
    back = np.arange(2 * P)[None, :]
    dist = r + P - back
    whole = lambda v: np.ascontiguousarray(np.broadcast_to(np.asarray(v).reshape(1, -1), (P, np.asarray(v).size)))
    by_pair = lambda v: whole(v.reshape(2, PAIRS).T).reshape(P, PAIRS, 2)
    xs = np.asarray(x)[0]
    return {
        "xT": np.ascontiguousarray(xs.T), "x": xs, "w_in": np.ascontiguousarray(tiles),
        "w_ba": np.ascontiguousarray(w_ba), "conv_w": np.ascontiguousarray(cw),
        "a_log": whole(a_log), "dt_bias": whole(dt_bias),
        "norm_w": np.ascontiguousarray(np.asarray(norm_w)[0].reshape(P, 1)), "sinks": by_pair(np.asarray(sinks)),
        "w_out": np.ascontiguousarray(wo), "ln_g": whole(ln_g), "ln_b": whole(ln_b),
        "c_tri": (r <= c).astype(np.float32), "c_ident": np.eye(P, dtype=np.float32),
        "c_masks": np.concatenate([first[:, None], levels], 1).astype(np.float32),
        "c_dist": np.where((dist >= 0) & (dist < P), -8.0 * dist, MASKED).astype(np.float32),
        "c_slope": by_pair(np.array([2.0 ** -(h + 1) for h in range(2 * PAIRS)], np.float32)),
    }


def kernel(**inputs):
    import concourse.bacc as bacc
    from concourse.bass_utils import run_bass_kernel_spmd

    arrays = layout(**inputs)
    nc = bacc.Bacc("TRN2", target_bir_lowering=False, num_devices=1, dynamic_dma_scratch_size=1024)
    args = [nc.dram_tensor(n, arrays[n].shape, mybir.dt.from_np(arrays[n].dtype), kind="ExternalInput").ap()
            for n in ORDER]
    y_spill = nc.dram_tensor("y_spill", (KT, P, T), F32, kind="Internal").ap()
    out = nc.dram_tensor("out", (T, D), F32, kind="ExternalOutput").ap()
    g_rows = nc.dram_tensor("g_rows", ((AH + 1) * NT, P), F32, kind="Internal").ap()
    build_layer(nc, *args, y_spill, g_rows, out)
    r = run_bass_kernel_spmd(nc, [arrays], core_ids=[0])
    return r.results[0]["out"].reshape(1, T, D)
```
